# Optimizing a Trainium2 kernel written in Bass

```python
import jax, jax.numpy as jnp
from jax import lax
import numpy as np

D_MODEL = 2048
BATCH = 1
SEQ = 256
DEPTH = 1

CHUNK = 64
EPS = 1e-6
RNN_DK = 128
RNN_DV = 128
RNN_HEADS = D_MODEL // RNN_DK
RNN_WIDTH = RNN_HEADS * RNN_DV
RNN_KWIDTH = RNN_HEADS * RNN_DK
ATT_HEAD_DIM = 64
ATT_HEADS = D_MODEL // ATT_HEAD_DIM
ATT_KV_HEADS = ATT_HEADS // 8
ATT_GROUP = ATT_HEADS // ATT_KV_HEADS
ATT_WIDTH = ATT_HEADS * ATT_HEAD_DIM
KV_WIDTH = ATT_KV_HEADS * ATT_HEAD_DIM
WINDOW = 128
WINDOW_CHUNKS = WINDOW // CHUNK
ROPE_THETA = 10000.0
D_FF = 4 * D_MODEL
PLE_DIM = 256
IN_SPLITS = (RNN_KWIDTH, RNN_KWIDTH, RNN_WIDTH, RNN_WIDTH,
             ATT_WIDTH, KV_WIDTH, KV_WIDTH,
             RNN_WIDTH, ATT_WIDTH)
IN_WIDTH = sum(IN_SPLITS)

kernel_name = "hybrid_hgrn2_swa_sink_block"

def rmsnorm(x, g):
    xf = x.astype(jnp.float32)
    y = xf * lax.rsqrt(jnp.mean(xf * xf, axis=-1, keepdims=True) + EPS)
    return (y * g.astype(jnp.float32)).astype(x.dtype)

def split_columns(z):
    idx = np.cumsum(np.array(IN_SPLITS))[:-1].tolist()
    return jnp.split(z, idx, axis=-1)

def rope_tables(positions):
    inv_freq = ROPE_THETA ** (-jnp.arange(0, ATT_HEAD_DIM, 2, dtype=jnp.float32) / ATT_HEAD_DIM)
    ang = positions.astype(jnp.float32)[..., None] * inv_freq
    return jnp.cos(ang)[:, :, None, :], jnp.sin(ang)[:, :, None, :]

def apply_rope(t, cos, sin):
    tf = t.astype(jnp.float32)
    t1, t2 = jnp.split(tf, 2, axis=-1)
    out = jnp.concatenate([t1 * cos - t2 * sin, t2 * cos + t1 * sin], axis=-1)
    return out.astype(t.dtype)

def hgrn2_mixer(q, f_logit, i_in, out_gate, lb, norm_g):
    B, S, _ = q.shape
    N = S // CHUNK
    f32 = jnp.float32
    qf = jax.nn.silu(q.astype(f32))
    f = lb + (1.0 - lb) * jax.nn.sigmoid(f_logit.astype(f32))
    k = 1.0 - f
    g = jnp.log(f)
    v = i_in.astype(f32)

    def to_chunks(t, d):
        return t.reshape(B, N, CHUNK, RNN_HEADS, d).transpose(1, 0, 3, 2, 4)

    qc, kc, vc, gc = to_chunks(qf, RNN_DK), to_chunks(k, RNN_DK), to_chunks(v, RNN_DV), to_chunks(g, RNN_DK)
    causal = jnp.tril(jnp.ones((CHUNK, CHUNK), dtype=bool))
    mid = CHUNK // 2 - 1

    def step(s_prev, inp):
        qn, kn, vn, gn = inp
        b = jnp.cumsum(gn, axis=-2)
        b_mid = b[..., mid:mid + 1, :]
        a = jnp.einsum('bhtd,bhsd->bhts', qn * jnp.exp(b - b_mid), kn * jnp.exp(b_mid - b))
        a = jnp.where(causal, a, 0.0)
        o = (jnp.einsum('bhts,bhsv->bhtv', a, vn)
             + jnp.einsum('bhtd,bhdv->bhtv', qn * jnp.exp(b), s_prev))
        b_last = b[..., -1:, :]
        s_new = (jnp.exp(b_last)[..., 0, :, None] * s_prev
                 + jnp.einsum('bhsd,bhsv->bhdv', kn * jnp.exp(b_last - b), vn))
        return s_new, o

    s0 = jnp.zeros((B, RNN_HEADS, RNN_DK, RNN_DV), f32)
    _, o = lax.scan(step, s0, (qc, kc, vc, gc))
    o = o.transpose(1, 0, 3, 2, 4).reshape(B, S, RNN_HEADS, RNN_DV)
    o = o * lax.rsqrt(jnp.mean(o * o, axis=-1, keepdims=True) + EPS) * norm_g.astype(f32)
    o = o.reshape(B, S, RNN_WIDTH) * jax.nn.silu(out_gate.astype(f32))
    return o.astype(q.dtype)

def band_blocks(t, n_chunks):
    parts = []
    for j in range(WINDOW_CHUNKS - 1, 0, -1):
        parts.append(jnp.pad(t, ((0, 0), (j, 0), (0, 0), (0, 0), (0, 0)))[:, :n_chunks])
    parts.append(t)
    return jnp.concatenate(parts, axis=2)

def swa_sink_attention(q, k, v, sinks, cos, sin):
    B, S, _ = q.shape
    N = S // CHUNK
    q = apply_rope(q.reshape(B, S, ATT_HEADS, ATT_HEAD_DIM), cos, sin)
    k = apply_rope(k.reshape(B, S, ATT_KV_HEADS, ATT_HEAD_DIM), cos, sin)
    v = v.reshape(B, S, ATT_KV_HEADS, ATT_HEAD_DIM)
    q = q.reshape(B, N, CHUNK, ATT_KV_HEADS, ATT_GROUP, ATT_HEAD_DIM)
    kb = band_blocks(k.reshape(B, N, CHUNK, ATT_KV_HEADS, ATT_HEAD_DIM), N)
    vb = band_blocks(v.reshape(B, N, CHUNK, ATT_KV_HEADS, ATT_HEAD_DIM), N)
    s = jnp.einsum('bnqhgd,bnkhd->bnhgqk', q, kb).astype(jnp.float32) * (ATT_HEAD_DIM ** -0.5)
    key_back = jnp.repeat(jnp.arange(WINDOW_CHUNKS - 1, -1, -1), CHUNK)
    valid = (jnp.arange(N)[:, None] - key_back[None, :]) >= 0
    s = jnp.where(valid[None, :, None, None, None, :], s, jnp.finfo(jnp.float32).min)
    sink = jnp.broadcast_to(sinks.astype(jnp.float32).reshape(ATT_KV_HEADS, ATT_GROUP)[None, None, :, :, None, None],
                            s.shape[:-1] + (1,))
    pr = jax.nn.softmax(jnp.concatenate([s, sink], axis=-1), axis=-1)[..., :-1].astype(v.dtype)
    o = jnp.einsum('bnhgqk,bnkhd->bnqhgd', pr, vb)
    return o.reshape(B, S, ATT_WIDTH)

def setup_inputs(seed: int = 0) -> dict:
    key = jax.random.key(seed)
    ks = jax.random.split(key, 16)
    f32 = jnp.float32
    nrm = lambda k, shape, scale: jax.random.normal(k, shape, f32) * scale
    x = jax.random.normal(ks[0], (BATCH, SEQ, D_MODEL), f32)
    p = jax.random.normal(ks[1], (DEPTH, BATCH, SEQ, PLE_DIM), f32)
    offset = jax.random.randint(ks[2], (BATCH,), 0, 4096, dtype=jnp.int32)
    positions = offset[:, None] + jnp.arange(SEQ, dtype=jnp.int32)[None, :]
    return {
        "x": x,
        "p": p,
        "positions": positions,
        "g_mix": 1.0 + nrm(ks[3], (DEPTH, D_MODEL), 0.02),
        "w_in": nrm(ks[4], (DEPTH, D_MODEL, IN_WIDTH), D_MODEL ** -0.5),
        "lb_logits": nrm(ks[5], (DEPTH + 1, RNN_KWIDTH), 0.1),
        "hgrn_norm_g": 1.0 + nrm(ks[6], (DEPTH, RNN_DV), 0.02),
        "sinks": nrm(ks[7], (DEPTH, ATT_HEADS), 0.5),
        "w_out": nrm(ks[8], (DEPTH, RNN_WIDTH + ATT_WIDTH, D_MODEL), (RNN_WIDTH + ATT_WIDTH) ** -0.5),
        "g_mlp": 1.0 + nrm(ks[9], (DEPTH, D_MODEL), 0.02),
        "w_up": nrm(ks[10], (DEPTH, D_MODEL, D_FF), D_MODEL ** -0.5),
        "w_down": nrm(ks[11], (DEPTH, D_FF, D_MODEL), D_FF ** -0.5),
        "w_ple_gate": nrm(ks[12], (DEPTH, D_MODEL, D_MODEL), D_MODEL ** -0.5),
        "w_ple_proj": nrm(ks[13], (DEPTH, PLE_DIM, D_MODEL), PLE_DIM ** -0.5),
        "g_final": 1.0 + nrm(ks[14], (D_MODEL,), 0.02),
    }

def reference(x, p, positions, g_mix, w_in, lb_logits, hgrn_norm_g, sinks, w_out,
              g_mlp, w_up, w_down, w_ple_gate, w_ple_proj, g_final):
    cos, sin = rope_tables(positions)
    lower_bounds = jnp.cumsum(jax.nn.softmax(lb_logits.astype(jnp.float32), axis=0), axis=0)
    for i in range(DEPTH):
        h = rmsnorm(x, g_mix[i])
        z = h @ w_in[i]
        q_r, f_r, i_r, og_r, q_a, k_a, v_a, gate_a, gate_b = split_columns(z)
        o_a = hgrn2_mixer(q_r, f_r, i_r, og_r, lower_bounds[i], hgrn_norm_g[i])
        o_b = swa_sink_attention(q_a, k_a, v_a, sinks[i], cos, sin)
        merged = jnp.concatenate([jax.nn.sigmoid(gate_a) * o_a, jax.nn.sigmoid(gate_b) * o_b], axis=-1)
        x = x + merged @ w_out[i]
        h = rmsnorm(x, g_mlp[i])
        x = x + jnp.square(jax.nn.relu(h @ w_up[i])) @ w_down[i]
        x = x + jax.nn.sigmoid(x @ w_ple_gate[i]) * (p[i] @ w_ple_proj[i])
    return rmsnorm(x, g_final)


_drawn_inputs = setup_inputs


def setup_inputs(seed=0):
    import zlib

    import numpy as np

    out = dict(_drawn_inputs(seed))
    spreads = {}
    factors = {'g_mix': 8.0,
     'lb_logits': 8.0,
     'hgrn_norm_g': 8.0,
     'sinks': 8.0,
     'g_mlp': 15.136,
     'g_final': 21.89,
     'w_ple_gate': 23.72,
     'p': 8.0,
     'w_ple_proj': 8.0}
    for name, (base, spread) in spreads.items():
        noise = np.random.default_rng([zlib.crc32(name.encode()), seed]).standard_normal(out[name].shape)
        drawn = base * np.exp(spread * noise) if base else spread * noise
        out[name] = __import__('jax').numpy.asarray(drawn.astype(out[name].dtype))
    for name, factor in factors.items():
        out[name] = (out[name] * factor).astype(out[name].dtype)
    return out
```

```python
from contextlib import ExitStack

import numpy as np

import concourse.bass as bass
from concourse import mybir

ALU = mybir.AluOpType
ACT = mybir.ActivationFunctionType
F32 = mybir.dt.float32
F32R = mybir.dt.float32r
I32 = mybir.dt.int32
U32 = mybir.dt.uint32
AX_X = mybir.AxisListType.X

P = 128
TT = 2
CHUNK = 64
COLS = 512
D_MODEL = 2048
KT = D_MODEL // P
HEADS = 16
NG = 4
HG = HEADS // NG
HD = 64
FF_GROUP = 1024
PLE = 256
EPS = 1e-6
THETA = 10000.0
E_MAX = 2.0 ** 63

Q0, F0, I0, OG0 = 0, 2048, 4096, 6144
QA0 = 8192
KV0 = QA0 + 2048
GA0 = KV0 + 512
GB0 = GA0 + 2048

RAW_SLOTS = 4
W_SLOTS = 4
LAG = 3
LOOP_CHUNKS = 64
LOOP_BLOCKS = 12
LOOP_TURNS = 8
ROUNDS = 3

TWO_PI = 2.0 * np.pi
C1 = float(np.round(TWO_PI * 2**9) / 2**9)
C2 = float(np.round((TWO_PI - C1) * 2**21) / 2**21)
C3 = float(np.float32(TWO_PI - C1 - C2))
ROUND_MAGIC = float(1.5 * 2**23)
PI_IN = 3.1415925


def blocks_before_loop():
    out = [("kv", 0, 0, range(8))]
    for j in range(NG):
        out += [(kind, j, 0, range(8)) for kind in ("qa", "gb", "f", "q")]
        if j:
            out += [("wo", j - 1, c, range(4)) for c in range(4)]
        out += [(kind, j, 0, range(8)) for kind in ("i", "og", "ga")]
    out += [("woa", NG - 1, c, range(2, 4)) for c in range(4)]
    out += [("wor", NG - 1, c, range(0, 2)) for c in range(4)]
    out += [("up", 0, b, range(8)) for b in range(2)]
    out += [("up", 1, b, range(8)) for b in range(2)]
    out += [("down", 0, c, range(4)) for c in range(4)]
    return out


def blocks_of_round():
    out = [("up", 2, b, range(8)) for b in range(2)]
    out += [("down", 1, c, range(4)) for c in range(4)]
    out += [("up", 3, b, range(8)) for b in range(2)]
    out += [("down", 2, c, range(4)) for c in range(4)]
    return out


def blocks_after_loop():
    out = [("down", 7, c, range(4)) for c in range(4)]
    for c in range(4):
        out += [("proj", 0, c, range(1)), ("gate", 0, c, range(8))]
    return out


def slots_of(blocks, n0, b0):
    out, n = [], n0
    for b, (kind, j, col, chunks) in enumerate(blocks):
        for c in chunks:
            out.append((n, b0 + b, kind, j, col, c, c == chunks[0], c == chunks[-1]))
            n += 1
    return out


HEAD = slots_of(blocks_before_loop(), 0, 0)
HEAD_CHUNKS, HEAD_BLOCKS = len(HEAD), len(blocks_before_loop())
BODY = slots_of(blocks_of_round(), HEAD_CHUNKS, HEAD_BLOCKS)
TAIL_CHUNKS0 = HEAD_CHUNKS + ROUNDS * LOOP_CHUNKS
TAIL_BLOCKS0 = HEAD_BLOCKS + ROUNDS * LOOP_BLOCKS
TAIL = slots_of(blocks_after_loop(), TAIL_CHUNKS0, TAIL_BLOCKS0)
assert len(BODY) == LOOP_CHUNKS and HEAD_CHUNKS % W_SLOTS == 0 and LOOP_BLOCKS % 2 == 0


def at(table, kind, j, col=0):
    return next(s[0] for s in table if s[2:5] == (kind, j, col))


def program(nc, x, p, positions, g_mix, w_in, lb_logits, hgrn_norm_g, sinks, w_out,
            g_mlp, w_up, w_down, w_ple_gate, w_ple_proj, g_final, out):
    with ExitStack() as ctx:
        def sb(name, shape, dt=F32):
            return ctx.enter_context(nc.sbuf_tensor(name, shape, dt))

        x_sb = sb("x_sb", [P, TT, D_MODEL])
        hT_hi = sb("hT_hi", [P, KT, TT, P], F32R)
        hT_lo = sb("hT_lo", [P, KT, TT, P], F32R)
        w_raw = sb("w_raw", [P, RAW_SLOTS, 2, COLS])
        w_hi = sb("w_hi", [P, W_SLOTS, 2, COLS], F32R)
        w_lo = sb("w_lo", [P, W_SLOTS, 2, COLS], F32R)
        mT_hi = sb("mT_hi", [P, 8, TT, P], F32R)
        mT_lo = sb("mT_lo", [P, 8, TT, P], F32R)
        ident = sb("ident", [P, P])
        rows = sb("rows", [P, P])
        cols = sb("cols", [P, P])
        lb = sb("lb", [P, HEADS])
        one_lb = sb("one_lb", [P, HEADS])
        sink_bc = sb("sink_bc", [P, 2 * HEADS])
        stat = sb("stat", [P, 64])
        cmask = sb("cmask", [P, 1, P])
        smask = sb("smask", [P, COLS])
        invf = sb("invf", [P, HD // 2])
        posi = sb("posi", [P, TT], I32)
        posf = sb("posf", [P, TT])
        cos = sb("cos", [P, TT, 32])
        sin = sb("sin", [P, TT, 32])
        tmp = sb("tmp", [P, 2, COLS])
        with ExitStack() as mix:
            def mb(name, shape, dt=F32):
                return mix.enter_context(nc.sbuf_tensor(name, shape, dt))

            za = mb("za", [P, TT, COLS])
            zb = mb("zb", [P, TT, COLS])
            val = mb("val", [P, TT, COLS])
            gate = mb("gate", [P, TT, COLS])
            eg = mb("eg", [P, TT, COLS])
            eg2 = mb("eg2", [P, TT, COLS])
            hf = mb("hf", [P, COLS])
            hk = mb("hk", [P, COLS])
            hg = mb("hg", [P, COLS])
            hb = mb("hb", [P, COLS])
            hd = mb("hd", [P, COLS])
            he = mb("he", [P, COLS])
            hq = mb("hq", [P, COLS])
            qe = mb("qe", [P, HG, TT * P])
            ebl = mb("ebl", [P, HG, 4])
            keA = mb("keA", [P, HG, TT, P])
            keB = mb("keB", [P, HG, 1, P])
            am = mb("am", [P, 2, 4, P])
            Sst = mb("Sst", [P, 3, HG, P])
            kTp = mb("kTp", [P, 4, 2, TT * P])
            vaug = mb("vaug", [P, TT, 4, HD + 1])
            qT = mb("qT", [P, 4, TT, P])
            pr0 = mb("pr0", [P, 2, P])
            pr1 = mb("pr1", [P, 2, 2 * P])
            pT = mb("pT", [P, 4, P])
            oa = mb("oa", [P, TT, 8, HD + 1])
            sgb = mb("sgb", [P, TT, COLS])
            asc = mb("asc", [P, 96])
        with ExitStack() as mlp:
            def lb_(name, shape, dt=F32):
                return mlp.enter_context(nc.sbuf_tensor(name, shape, dt))

            u_sb = lb_("u_sb", [P, 2, TT, COLS])
            aT_hi = lb_("aT_hi", [P, 8, TT, P], F32R)
            aT_lo = lb_("aT_lo", [P, 8, TT, P], F32R)
            pj = lb_("pj", [P, TT, D_MODEL])
            gf_bc = lb_("gf_bc", [P, D_MODEL])
            pe_sb = lb_("pe_sb", [P, TT, PLE])
            pT_hi = lb_("pT_hi", [P, 2, TT, P], F32R)
            pT_lo = lb_("pT_lo", [P, 2, TT, P], F32R)
            eple = lb_("eple", [P, TT, COLS])

        acc = [[ctx.enter_context(nc.psum_tensor(f"acc{b}{t}", [P, COLS], F32)) for t in range(TT)]
               for b in range(2)]
        T = [ctx.enter_context(nc.psum_tensor(f"turn{i}", [P, COLS], F32)) for i in range(4)]

        def sem(name):
            return ctx.enter_context(nc.semaphore(name))

        x_landed = [[sem(f"x_landed{t}{half}") for half in range(2)] for t in range(TT)]
        rows_filled = sem("rows_filled")
        rows_landed = sem("rows_landed")
        sinks_landed = sem("sinks_landed")
        pos_landed = sem("pos_landed")
        gf_landed = sem("gf_landed")
        p_landed = sem("p_landed")
        ident_made = sem("ident_made")
        masks_made = sem("masks_made")
        invf_made = sem("invf_made")
        zeroed = sem("zeroed")
        w_landed = [sem(f"w_landed{s}") for s in range(RAW_SLOTS)]
        w_hi_ready = sem("w_hi_ready")
        w_lo_ready = sem("w_lo_ready")
        w_used = sem("w_used")
        turn_full = [sem(f"turn_full{b}") for b in range(4)]
        ss_ready = sem("ss_ready")
        rs_v = sem("rs_v")
        rs_y = sem("rs_y")
        r_ready = sem("r_ready")
        angles_ready = sem("angles_ready")
        trig_ready = sem("trig_ready")
        cols_ready = sem("cols_ready")
        lbd_ready = sem("lbd_ready")
        lb_exp = sem("lb_exp")
        tmp_full = sem("tmp_full")
        hi_done = sem("hi_done")
        hT_ready = sem("hT_ready")
        kv_out = sem("kv_out")
        qa_out = sem("qa_out")
        gb_exp = sem("gb_exp")
        gb_bounded = sem("gb_bounded")
        gb_sig = sem("gb_sig")
        f_out = sem("f_out")
        q_out = sem("q_out")
        i_out = sem("i_out")
        og_exp = sem("og_exp")
        og_out = sem("og_out")
        ga_exp = sem("ga_exp")
        og_bounded = sem("og_bounded")
        ga_bounded = sem("ga_bounded")
        gate_logs = sem("gate_logs")
        logs_added = sem("logs_added")
        gate_sig = sem("gate_sig")
        rope_products = sem("rope_products")
        k_rotated = sem("k_rotated")
        qa_rotated = sem("qa_rotated")
        kTp_out = sem("kTp_out")
        qaT_out = sem("qaT_out")
        nm_ready = sem("nm_ready")
        pr_ready = sem("pr_ready")
        pT_out = sem("pT_out")
        pv_out = sem("pv_out")
        sinkd_ready = sem("sinkd_ready")
        sink_exp = sem("sink_exp")
        am_ready = sem("am_ready")
        moA_hi = sem("moA_hi")
        moA_ready = sem("moA_ready")
        f_exp = sem("f_exp")
        f_bounded = sem("f_bounded")
        f_sig = sem("f_sig")
        f_ready = sem("f_ready")
        g_ready = sem("g_ready")
        b_ready = sem("b_ready")
        q_exp = sem("q_exp")
        q_bounded = sem("q_bounded")
        q_sig = sem("q_sig")
        q_ready = sem("q_ready")
        decays = sem("decays")
        qkd_ready = sem("qkd_ready")
        qe_ready = sem("qe_ready")
        bend_ready = sem("bend_ready")
        eend_ready = sem("eend_ready")
        ke_ready = sem("ke_ready")
        ke_out = sem("ke_out")
        am_masked = sem("am_masked")
        S_ready = sem("S_ready")
        o_squared = sem("o_squared")
        gated = sem("gated")
        mo_ready = sem("mo_ready")
        mo_weighted = sem("mo_weighted")
        moR_hi = sem("moR_hi")
        moR_ready = sem("moR_ready")
        x_added = sem("x_added")
        u_ready = sem("u_ready")
        squared = sem("squared")
        a_hi = sem("a_hi")
        aT_ready = sem("aT_ready")
        pp_hi = sem("pp_hi")
        ppT_ready = sem("ppT_ready")
        proj_out = sem("proj_out")
        gate_out = sem("gate_out")
        x3_ready = sem("x3_ready")
        x3_scaled = sem("x3_scaled")
        last_ready = sem("last_ready")
        out_ready = sem("out_ready")
        out_stored = sem("out_stored")

        def count(value, r=0, per=0):
            return value + r * per

        before, body, after = blocks_before_loop(), blocks_of_round(), blocks_after_loop()
        number = {(kind, j, col): b for b, (kind, j, col, _) in enumerate(before + body)}
        number.update({(kind, j, col): TAIL_BLOCKS0 + b for b, (kind, j, col, _) in enumerate(after)})
        last_chunk = {s[2:5]: s[0] for s in HEAD + BODY + TAIL if s[7]}
        order = [x[:3] for x in before + body]

        def block_before(b, back):
            b -= back
            if b < len(order):
                return order[b]
            i = b - TAIL_BLOCKS0
            if i >= 0:
                return after[i][:3]
            kind, j, col = order[i]
            return kind, j + 2 * (ROUNDS - 1), col

        def added_index(kind, j, col):
            return {"wo": 4 * j, "woa": 12, "wor": 16, "down": 20 + 4 * j}[kind] + col

        def left_psum(b, r=0):
            kind, j, col = block_before(b, 0)
            if kind in ("wo", "woa", "wor", "down"):
                return x_added, count(2 * (added_index(kind, j, col) + 1), r, 16)
            if kind == "up":
                return u_ready, count(2 * (2 * j + col + 1), r, 8)
            if kind in ("proj", "gate"):
                return (proj_out if kind == "proj" else gate_out), 2 * (col + 1)
            signal = {"kv": kv_out, "qa": qa_out, "gb": gb_exp, "f": f_out, "q": q_out, "i": i_out,
                      "og": og_out, "ga": ga_exp}[kind]
            return signal, 2 * (j + 1)

        def product(kind, j, col, r=0):
            return count(last_chunk[(kind, j, col)] + 1, r, LOOP_CHUNKS)

        def acc_of(kind, j, col, t):
            return acc[number[(kind, j, col)] % 2][t]

        jobs = [[], [], [], []]
        uses = {}
        read_by = {}

        def use(name, bank, signal, value, extra=0):
            uses[name] = (bank, len(jobs[bank]) + extra)
            read_by[name] = (signal, value)
            jobs[bank].append(name)

        use(("rows",), 3, cols_ready, 1)
        for cb in range(4):
            for t in range(TT):
                use(("xT", cb, t), t + 2 * (cb % 2), tmp_full, 2 * cb + t + 1)
        for i in range(4):
            use(("kT", i), i, kTp_out, i + 1)
        for j in range(NG):
            for t in range(TT):
                use(("qaT", j, t), t, qaT_out, 2 * j + t + 1)
            for u in range(8):
                use(("score", j, u), 0, pr_ready, 8 * j + u + 1)
                use(("pT", j, u), 1, pT_out, 8 * j + u + 1)
                use(("pv", j, u), 1, pv_out, 8 * j + u + 1)
            for t in range(TT):
                use(("amT", j, t), t, moA_ready, 2 * j + t + 1)
            for hp in range(2):
                use(("fT", j, hp), 2, f_exp, 2 * j + hp + 1)
                use(("qT", j, hp), 3, q_ready, 2 * j + hp + 1)
                use(("keT", j, hp), 2, ke_out, 2 * (2 * j + hp + 1))
                use(("aT", j, hp), 3, am_masked, 2 * j + hp + 1)
            for c in range(3):
                use(("state", j, c), 2 + c % 2, S_ready, 12 * j + 4 * (c + 1))
            for t in range(TT):
                use(("o", j, t), 3 - t, mo_ready, 2 * j + t + 1)
            for t in range(TT):
                use(("moT", j, t), 3 - t, mo_weighted, 2 * j + t + 1)
        for cb in range(4):
            for t in range(TT):
                use(("x1T", cb, t), t + 2 * (cb % 2), tmp_full, 8 + 2 * cb + t + 1)
        for g in range(4):
            for b in range(2):
                for t in range(TT):
                    use(("uT", g, b, t), 2 * b + t, squared, 2 * (2 * g + b) + t + 1)
        per_bank = LOOP_TURNS // 4
        skipped = (ROUNDS - 1) * per_bank
        for t in range(TT):
            use(("ppT", t), t, ppT_ready, t + 1, skipped)
        for cb in range(4):
            for t in range(TT):
                use(("x2T", cb, t), t + 2 * (cb % 2), hT_ready, 16 + 2 * cb + t + 1, skipped)

        def bank(name):
            return T[uses[name][0]]

        def bank_free(name, r=0):
            seq = jobs[uses[name][0]]
            former = seq[seq.index(name) - 1]
            if former[0] == "uT" and name[0] != "uT":
                return squared, 2 * (2 * 7 + former[2]) + former[3] + 1
            signal, value = read_by[former]
            return signal, count(value, r, LOOP_TURNS)

        def full(name):
            return turn_full[uses[name][0]]

        def nth(name, r=0):
            return count(uses[name][1] + 1, r, per_bank)

        class Chain:

            def __init__(self, eng, name):
                self.eng, self.sem, self.n = eng, sem(name), 0

            def __call__(self, ins):
                self.n += 1
                ins.then_inc(self.sem, 1)
                self.eng.wait_ge(self.sem, self.n)

        KV1 = 8
        A0 = [at(HEAD, "gb", j) + 8 for j in range(NG)]
        H0 = [at(HEAD, "f", j) for j in range(NG)]
        WOR = at(HEAD, "wor", NG - 1)
        UP0 = at(HEAD, "up", 0)
        DOWN7 = at(TAIL, "down", 7)
        PROJ = [at(TAIL, "proj", 0, c) for c in range(4)]
        I_END, OG_END, GA_END = ([at(HEAD, kind, j) + 8 - H0[j] for j in range(NG)] for kind in ("i", "og", "ga"))
        UNIT = 4
        ATT_END = UNIT * 7 + 11
        F_TURN, Q_TURN, DECAY, KE_TURN = (9, 26), (17, 28), (20, 35), (25, 40)
        SS, V, Y, R, NR = 0, 8, 10, 12, 14
        HV, HY, HR, HW = 16, 24, 32, 40
        NM, SD, DEN, MX = 0, 16, 32, 48

        OUT_PARTS = [(0, 0), (0, 1), (1, 0)]
        HALF = CHUNK // 2
        HALVES = [(0, CHUNK), (HALF, HALF), (CHUNK, CHUNK), (CHUNK + HALF, HALF)]

        def keys_of(t):
            return (0, P) if t == 0 else (CHUNK, 3 * CHUNK)

        def four(ap):
            return ap.rearrange("p (k c) -> p k c", k=4)

        block = ctx.enter_context(nc.Block())

        @block.sync
        def _(sp):
            sp.dma_start(rows[0:16, :], g_mix[0].rearrange("(h p) -> h p", p=P)).then_inc(rows_landed, 16)
            sp.dma_start(rows[16:32, :], g_mlp[0].rearrange("(h p) -> h p", p=P)).then_inc(rows_landed, 16)

            def load_x(half):
                hs = slice(half * 1024, (half + 1) * 1024)
                for t in range(TT):
                    sp.dma_start(x_sb[:, t, hs], x[0, t * P:(t + 1) * P, hs]).then_inc(x_landed[t][half], 16)

            load_x(0)

            def view(w):
                return w.rearrange("(k p) n -> p k n", p=P)

            wi, wo, wu, wd = view(w_in[0]), view(w_out[0]), view(w_up[0]), view(w_down[0])
            wg, wp = view(w_ple_gate[0]), view(w_ple_proj[0])
            in_cols = {"kv": KV0, "qa": QA0, "gb": GB0, "f": F0, "q": Q0, "i": I0, "og": OG0, "ga": GA0}

            def load(slot, r=0):
                n, _, kind, j, col, c, _, _ = slot
                cs = slice(col * COLS, (col + 1) * COLS)
                if kind in in_cols:
                    c0 = in_cols[kind] + j * COLS
                    src = wi[:, 2 * c:2 * c + 2, c0:c0 + COLS]
                elif kind in ("wo", "woa", "wor"):
                    k0 = (4 * j if c < 2 else KT + 4 * j) + 2 * (c % 2)
                    src = wo[:, k0:k0 + 2, cs]
                elif kind == "up":
                    c0 = j * FF_GROUP + col * COLS
                    src = wu[:, 2 * c:2 * c + 2, bass.ds(r * (2 * FF_GROUP) + c0, COLS)]
                elif kind == "down":
                    src = wd[:, bass.ds(r * 16 + (8 * j + 2 * c), 2), cs]
                elif kind == "gate":
                    src = wg[:, 2 * c:2 * c + 2, cs]
                else:
                    src = wp[:, 0:2, cs]
                if n >= RAW_SLOTS:
                    sp.wait_ge(w_lo_ready, count(n - RAW_SLOTS + 1, r, LOOP_CHUNKS))
                sp.dma_start(w_raw[:, n % RAW_SLOTS], src).then_inc(w_landed[n % RAW_SLOTS], 16)

            for slot in HEAD:
                if slot[0] == 2:
                    load_x(1)
                load(slot)
            with sp.Fori(0, ROUNDS) as r:
                for slot in BODY:
                    load(slot, r)
            for slot in TAIL:
                load(slot)
            for i, (t, half) in enumerate(OUT_PARTS):
                sp.wait_ge(out_ready, i + 1)
                hs = slice(half * 1024, (half + 1) * 1024)
                sp.dma_start(out[0, t * P:(t + 1) * P, hs], x_sb[:, t, hs]).then_inc(out_stored, 16)
            sp.wait_ge(out_stored, 16 * 4)

        @block.gpsimd
        def _(pool):
            chain = Chain(pool, "pool_chain")
            pool.memset(rows[64:P, :], 0.0).then_inc(rows_filled, 1)
            pool.wait_ge(rows_filled, 1)
            chain(pool.memset(ident[:], 0.0))
            pool.affine_select(out=ident[:], in_=ident[:], compare_op=ALU.not_equal, fill=1.0, base=0,
                               pattern=[[-1, P]], channel_multiplier=1).then_inc(ident_made, 1)
            inv = np.float32(THETA) ** (-np.arange(0, HD, 2, dtype=np.float32) / np.float32(HD))
            for i in range(HD // 2):
                pool.memset(invf[:, i:i + 1], float(inv[i])).then_inc(invf_made, 1)
            for b in (gate, eg, pr0, pr1, keA, keB, am):
                pool.memset(b[:], 0.0).then_inc(zeroed, 1)
            pool.memset(vaug[:, :, :, HD:HD + 1], 1.0).then_inc(zeroed, 1)
            chain(pool.memset(cmask[:], 1.0))
            chain(pool.affine_select(out=cmask[:, 0, :], in_=cmask[:, 0, :], compare_op=ALU.is_ge, fill=0.0, base=0,
                                     pattern=[[1, P]], channel_multiplier=-1))
            pool.affine_select(out=cmask[:, 0, CHUNK:], in_=cmask[:, 0, CHUNK:], compare_op=ALU.is_ge,
                               fill=0.0, base=-CHUNK, pattern=[[0, CHUNK]],
                               channel_multiplier=1).then_inc(masks_made, 1)
            chain(pool.memset(smask[:], 1.0))
            pool.memset(smask[:].rearrange("p (s c) -> p s c", c=CHUNK)[:, :, 0:1], 0.0)\
                .then_inc(masks_made, 1)

        @block.tensor
        def _(pe):
            parts = {"h": (hT_hi, hT_lo), "m": (mT_hi, mT_lo), "a": (aT_hi, aT_lo), "p": (pT_hi, pT_lo)}

            def stationary(kind, j):
                if kind in ("wo", "woa", "wor"):
                    return parts["m"]
                if kind == "down":
                    return parts["a" if j % 2 == 0 else "m"]
                return parts["p" if kind == "proj" else "h"]

            def chunk(slot, r=0):
                n, b, kind, j, col, c, first, last = slot
                hi, lo = stationary(kind, j)
                if first:
                    if b >= 2:
                        signal, value = left_psum(b - 2, r)
                        pe.wait_ge(signal, value)
                    if col == 0:
                        stationary_ready(kind, j, r)
                if kind == "kv" and c % 2 == 0:
                    pe.wait_ge(hT_ready, 2 * (c // 2 + 1))
                if kind == "up" and j == 0 and col == 0 and c % 2 == 0:
                    pe.wait_ge(hT_ready, 8 + 2 * (c // 2 + 1))
                if kind == "gate" and col == 0 and c % 2 == 0:
                    pe.wait_ge(hT_ready, 16 + 2 * (c // 2 + 1))
                pe.wait_ge(w_lo_ready, count(n + 1, r, LOOP_CHUNKS))
                s = n % W_SLOTS
                for kk in range(2):
                    k = 2 * c + kk
                    for t in range(TT):
                        a = acc[b % 2][t][:]
                        pe.matmul(a, hi[:, k, t, :], w_hi[:, s, kk, :], start=first and kk == 0, stop=False)
                        pe.matmul(a, hi[:, k, t, :], w_lo[:, s, kk, :], start=False, stop=False)
                        mm = pe.matmul(a, lo[:, k, t, :], w_hi[:, s, kk, :], start=False,
                                       stop=last and kk == 1)
                mm.then_inc(w_used, 1)

            def stationary_ready(kind, j, r):
                if kind in ("wo", "woa"):
                    pe.wait_ge(moA_ready, 2 * (j + 1))
                if kind in ("wo", "wor"):
                    pe.wait_ge(moR_ready, 2 * (j + 1))
                if kind == "down":
                    pe.wait_ge(aT_ready, count(4 * (j + 1), r, LOOP_TURNS))
                if kind == "proj":
                    pe.wait_ge(ppT_ready, 2)

            def turn(name, src, r=0):
                if uses[name][1] > 0:
                    signal, value = bank_free(name, r)
                    pe.wait_ge(signal, value)
                for i in range(4):
                    mm = pe.transpose(bank(name)[:, i * P:(i + 1) * P], src(i), ident[:])
                mm.then_inc(full(name), 1)

            def x_turn(stage, cb, t):
                turn((stage, cb, t), lambda i: x_sb[:, t, (4 * cb + i) * P:(4 * cb + i + 1) * P])

            def head_turn(kind, j, hp, src):
                turn((kind, j, hp), lambda i: src[:, i % 2, (2 * hp + i // 2) * P:(2 * hp + i // 2 + 1) * P])

            def scores(j, u, t, pair):
                name = ("score", j, u)
                if u == 0:
                    pe.wait_ge(qaT_out, 2 * (j + 1))
                    pe.wait_ge(kTp_out, 4)
                signal, value = bank_free(name)
                pe.wait_ge(signal, value)
                k0, nk = keys_of(t)
                mm = pe.matmul(bank(name)[:, 0:2 * nk].rearrange("p (v k) -> p v k", v=2),
                               qT[:, pair, t, :], kTp[:, j, :, k0:k0 + nk], start=True, stop=True)
                mm.then_inc(full(name), 1)

            def weights_turn(j, u, t):
                name = ("pT", j, u)
                pe.wait_ge(pr_ready, 8 * j + u + 1)
                signal, value = bank_free(name)
                pe.wait_ge(signal, value)
                for hh in range(2):
                    for kt in range(t + 1):
                        i = hh * (t + 1) + kt
                        src = pr0[:, hh, :] if t == 0 else pr1[:, hh, kt * P:(kt + 1) * P]
                        mm = pe.transpose(bank(name)[:, i * P:(i + 1) * P], src, ident[:])
                mm.then_inc(full(name), 1)

            def weighted_values(j, u, t):
                name = ("pv", j, u)
                pe.wait_ge(pT_out, 8 * j + u + 1)
                signal, value = bank_free(name)
                pe.wait_ge(signal, value)
                for hh in range(2):
                    for kt in range(t + 1):
                        mm = pe.matmul(bank(name)[:, hh * (HD + 1):(hh + 1) * (HD + 1)],
                                       pT[:, hh * (t + 1) + kt, :], vaug[:, kt, j, :],
                                       start=kt == 0, stop=kt == t)
                mm.then_inc(full(name), 1)

            def recurrence_scores(j, hp):
                name = ("aT", j, hp)
                pe.wait_ge(qkd_ready, 2 * j + hp + 1)
                signal, value = bank_free(name)
                pe.wait_ge(signal, value)
                for i in range(4):
                    for s0, nt in HALVES:
                        mm = pe.matmul(bank(name)[s0:s0 + HALF, i * P + s0:i * P + s0 + nt],
                                       hd[:, i * P + s0:i * P + s0 + HALF],
                                       he[:, i * P + s0:i * P + s0 + nt], start=True, stop=True,
                                       skip_group_check=True)
                mm.then_inc(full(name), 1)

            def states(j, chunks):
                pe.wait_ge(ke_out, 4 * (j + 1))
                pe.wait_ge(i_out, 2 * (j + 1))
                for c in chunks:
                    name = ("state", j, c)
                    signal, value = bank_free(name)
                    pe.wait_ge(signal, value)
                    ke = keA if c % 2 == 0 else keB
                    for h in range(HG):
                        mm = pe.matmul(bank(name)[:, h * P:(h + 1) * P], ke[:, h, c // 2, :],
                                       val[:, c // 2, h * P:(h + 1) * P], start=True, stop=True)
                    mm.then_inc(full(name), 1)

            def outputs(j):
                pe.wait_ge(am_masked, 2 * (j + 1))
                for t in range(TT):
                    name = ("o", j, t)
                    signal, value = bank_free(name)
                    pe.wait_ge(signal, value)
                    pe.wait_ge(S_ready, 12 * j + (4 if t == 0 else 12))
                    for h in range(HG):
                        o = bank(name)[:, h * P:(h + 1) * P]
                        mm = pe.matmul(o, am[:, h // 2, (h % 2) * 2 + t, :], val[:, t, h * P:(h + 1) * P],
                                       start=True, stop=False, skip_group_check=True)
                        for half in range(2):
                            c = 2 * t + half
                            if c > 0:
                                mm = pe.matmul(o[half * CHUNK:(half + 1) * CHUNK, :],
                                               qe[:, h, c * CHUNK:(c + 1) * CHUNK], Sst[:, c - 1, h, :],
                                               start=False, stop=True, skip_group_check=True)
                    mm.then_inc(full(name), 1)

            def steps(n):
                if n == KV1 + 5:
                    for i in range(4):
                        t, half = divmod(i, 2)
                        pe.wait_ge(k_rotated, t + 1)
                        src = (gate if t == 0 else eg)[:].rearrange("p a b -> p (a b)")
                        turn(("kT", i), lambda q: src[:, (4 * half + q) * P:(4 * half + q + 1) * P])
                for j in range(NG):
                    a, h = n - A0[j], n - H0[j]
                    if a == -3:
                        for t in range(TT):
                            pe.wait_ge(qa_rotated, 2 * j + t + 1)
                            turn(("qaT", j, t), lambda i: zb[:, t, i * P:(i + 1) * P])
                    for u in range(8):
                        t, pair = divmod(u, 4)
                        if a == UNIT * u + 4:
                            scores(j, u, t, pair)
                        if a == UNIT * u + 7:
                            weights_turn(j, u, t)
                        if a == UNIT * u + 9:
                            weighted_values(j, u, t)
                    if a == ATT_END + 4:
                        for t in range(TT):
                            pe.wait_ge(am_ready, 2 * j + t + 1)
                            turn(("amT", j, t), lambda i: sgb[:, t, i * P:(i + 1) * P])
                    for hp in range(2):
                        if h == F_TURN[hp]:
                            pe.wait_ge(f_out, 2 * (j + 1))
                            head_turn("fT", j, hp, za)
                        if h == Q_TURN[hp]:
                            pe.wait_ge(q_out, 2 * (j + 1))
                            head_turn("qT", j, hp, zb)
                        if h == KE_TURN[hp]:
                            pe.wait_ge(ke_ready, 2 * j + hp + 1)
                            turn(("keT", j, hp), lambda i: hf[:, i * P:(i + 1) * P])
                            recurrence_scores(j, hp)
                    if h == 42:
                        states(j, (0, 1))
                    if h == 44:
                        states(j, (2,))
                    if h == 47:
                        outputs(j)
                    if h == 61:
                        for t in range(TT):
                            pe.wait_ge(mo_ready, 2 * j + t + 1)
                            turn(("moT", j, t), lambda i: gate[:, t, i * P:(i + 1) * P])
                for cb in range(4):
                    if n == WOR + 2 * (cb + 1) + 1:
                        pe.wait_ge(x_added, 2 * (added_index("wor", 3, cb) + 1))
                        for t in range(TT):
                            x_turn("x1T", cb, t)

            def up_turn(slot, r=0):
                kind, j, col = block_before(slot[1], 1)
                if kind == "up" and slot[5] == 2:
                    for t in range(TT):
                        pe.wait_ge(u_ready, count(2 * (2 * j + col) + t + 1, r, 8))
                        turn(("uT", j, col, t), lambda i: u_sb[:, col, t, i * P:(i + 1) * P], r)

            pe.wait_ge(ident_made, 1)
            pe.wait_ge(rows_landed, 16 * 4)
            pe.transpose(bank(("rows",))[:, 0:P], rows[:], ident[:]).then_inc(full(("rows",)), 1)
            for slot in HEAD:
                n = slot[0]
                for cb in range(4):
                    if n == max(0, 2 * cb - 2):
                        for t in range(TT):
                            pe.wait_ge(x_landed[t][cb // 2], 16)
                            x_turn("xT", cb, t)
                chunk(slot)
                steps(n)
                if n >= UP0:
                    up_turn(slot)
            with pe.Fori(0, ROUNDS) as r:
                for slot in BODY:
                    chunk(slot, r)
                    up_turn(slot, r)
            for slot in TAIL:
                n = slot[0]
                chunk(slot)
                if n == DOWN7:
                    pe.wait_ge(p_landed, 16)
                    for t in range(TT):
                        name = ("ppT", t)
                        signal, value = bank_free(name)
                        pe.wait_ge(signal, value)
                        for k in range(2):
                            mm = pe.transpose(bank(name)[:, k * P:(k + 1) * P],
                                              pe_sb[:, t, k * P:(k + 1) * P], ident[:])
                        mm.then_inc(full(name), 1)
                for cb in range(4):
                    if n == DOWN7 + 4 * (cb + 1) + 1:
                        pe.wait_ge(x_added, 2 * (added_index("down", 7, cb) + 1))
                        for t in range(TT):
                            x_turn("x2T", cb, t)

        @block.scalar
        def _(act):
            chain = Chain(act, "act_chain")
            with nc.allow_non_contiguous_dma(reason="256 positions"):
                act.dma_start(posi[:], positions[0].rearrange("(t p) -> p t", p=P)).then_inc(pos_landed, 16)
            act.dma_start(rows[32:64, :], lb_logits.rearrange("a (h p) -> (a h) p", p=P)).then_inc(rows_landed, 16)
            act.wait_ge(rows_filled, 1)
            act.dma_start(rows[64:65, :], hgrn_norm_g).then_inc(rows_landed, 16)
            act.dma_start(sink_bc[:], sinks[0].partition_broadcast(P)).then_inc(sinks_landed, 16)
            nc.scalar.preload_act_table_set("trig_and_small")

            def rope_sines():
                act.wait_ge(angles_ready, 1)
                act.activation(sin[:], sgb[:, 0, 0:64].rearrange("p (t i) -> p t i", t=TT), ACT.Sin)\
                   .then_inc(trig_ready, 1)
                act.activation(cos[:], sgb[:, 0, 64:128].rearrange("p (t i) -> p t i", t=TT), ACT.Sin)\
                   .then_inc(trig_ready, 1)
                nc.scalar.preload_act_table_set("natural_log_exp_and_others")

            def split_hi(slot, r=0):
                n = slot[0]
                act.wait_ge(w_landed[n % RAW_SLOTS], count(16 * (n // RAW_SLOTS + 1), r, 16 * LOOP_CHUNKS // RAW_SLOTS))
                if n >= W_SLOTS:
                    act.wait_ge(w_used, count(n - W_SLOTS + 1, r, LOOP_CHUNKS))
                act.activation(w_hi[:, n % W_SLOTS], w_raw[:, n % RAW_SLOTS], ACT.Copy)\
                   .then_inc(w_hi_ready, 1)

            def sum_squares(t, stage, squares):
                for half in range(2):
                    if stage == 0:
                        act.wait_ge(x_landed[t][half], 16)
                    act.activation(squares, x_sb[:, t, half * 1024:(half + 1) * 1024], ACT.Square,
                                   accum_out=stat[:, SS + 2 * t + half:SS + 2 * t + half + 1])\
                       .then_inc(ss_ready, 1)
                    act.wait_ge(ss_ready, 4 * stage + 2 * t + half + 1)

            def rsqrt_start(which, v, y, width):
                act.wait_ge(rs_v, which + 1)
                chain(act.activation(stat[:, y:y + width], stat[:, v:v + width], ACT.Ln))
                act.activation(stat[:, y:y + width], stat[:, y:y + width], ACT.Exp, scale=-0.5)\
                   .then_inc(rs_y, 1)

            def x_hi(stage, cb, t):
                i = 8 * stage + 2 * cb + t
                act.wait_ge(tmp_full, i + 1)
                act.activation(hT_hi[:, 4 * cb:4 * cb + 4, t, :], four(tmp[:, t]), ACT.Copy)\
                   .then_inc(hi_done, 1)

            def z_out(kind, j, dst, done, func=ACT.Copy, scale=R):
                act.wait_ge(w_used, product(kind, j, 0))
                if j == 0:
                    act.wait_ge(r_ready, 1)
                for t in range(TT):
                    act.activation(dst[:, t], acc_of(kind, j, 0, t)[:], func,
                                   scale=stat[:, scale + t:scale + t + 1]).then_inc(done, 1)

            def exponentials(j, u, t, pair):
                name = ("score", j, u)
                act.wait_ge(full(name), nth(name))
                act.wait_ge(nm_ready, 8 * j + u + 1)
                act.wait_ge(zeroed, 8)
                if u:
                    act.wait_ge(pT_out, 8 * j + u)
                k0, nk = keys_of(t)
                for half in range(2):
                    rows_ = slice(half * CHUNK, (half + 1) * CHUNK)
                    first = max(0, (2 * t + half - 1) * CHUNK)
                    keys = (2 * t + half + 1) * CHUNK - first
                    for hh in range(2):
                        head = t * 8 + 2 * pair + hh
                        dst = (pr0 if t == 0 else pr1)[rows_, hh, first:first + keys]
                        s0 = hh * nk + first - k0
                        ins = act.activation(dst, bank(name)[rows_, s0:s0 + keys], ACT.Exp, scale=HD ** -0.5,
                                             bias=asc[rows_, NM + head:NM + head + 1])
                ins.then_inc(pr_ready, 1)

            def steps(n):
                for t in range(TT):
                    if n == t + 3:
                        sum_squares(t, 0, za[:].rearrange("p a b -> p (a b)"))
                if n == 0:
                    rope_sines()
                if n == 5:
                    rsqrt_start(0, V, Y, TT)
                    act.wait_ge(lbd_ready, 1)
                    act.activation(asc[:, 16:48], asc[:, 16:48], ACT.Exp).then_inc(lb_exp, 1)
                if n == KV1:
                    act.wait_ge(w_used, product("kv", 0, 0))
                    act.wait_ge(r_ready, 1)
                    act.wait_ge(zeroed, 8)
                    for t in range(TT):
                        a = acc_of("kv", 0, 0, t)
                        rcol = stat[:, R + t:R + t + 1]
                        chain(act.activation(vaug[:, t, :, 0:HD], four(a[:, 256:512]), ACT.Copy, scale=rcol))
                        act.activation(eg2[:, t, 0:256], a[:, 0:256], ACT.Copy, scale=rcol).then_inc(kv_out, 1)
                if n == KV1 + 6:
                    for i in range(4):
                        t, half = divmod(i, 2)
                        act.wait_ge(full(("kT", i)), nth(("kT", i)))
                        act.activation(kTp[:, 2 * half:2 * half + 2, :, t * P:(t + 1) * P],
                                       bank(("kT", i))[:].rearrange("p (h v c) -> p h v c", h=2, v=2),
                                       ACT.Copy).then_inc(kTp_out, 1)
                for j in range(NG):
                    a, h = n - A0[j], n - H0[j]
                    if a == -8:
                        z_out("qa", j, za, qa_out)
                    if a == -2:
                        for t in range(TT):
                            act.wait_ge(full(("qaT", j, t)), nth(("qaT", j, t)))
                            act.activation(qT[:, :, t, :], four(bank(("qaT", j, t))[:]), ACT.Copy)\
                               .then_inc(qaT_out, 1)
                    if a == 0:
                        z_out("gb", j, sgb, gb_exp, ACT.Exp, NR)
                    if a == 1:
                        for t in range(TT):
                            act.wait_ge(gb_bounded, 2 * j + t + 1)
                            chain(act.activation(sgb[:, t], sgb[:, t], ACT.Ln, bias=1.0))
                            act.activation(sgb[:, t], sgb[:, t], ACT.Exp, scale=-1.0).then_inc(gb_sig, 1)
                    for u in range(8):
                        if a == UNIT * u + 5:
                            exponentials(j, u, *divmod(u, 4))
                    if a == ATT_END + 1:
                        act.wait_ge(sinkd_ready, j + 1)
                        act.activation(asc[:, SD:SD + 16], asc[:, SD:SD + 16], ACT.Exp).then_inc(sink_exp, 1)
                    if a == ATT_END + 5:
                        for t in range(TT):
                            act.wait_ge(full(("amT", j, t)), nth(("amT", j, t)))
                            act.activation(mT_hi[:, 4:8, t, :], four(bank(("amT", j, t))[:]), ACT.Copy)\
                               .then_inc(moA_hi, 1)
                    if h == 8:
                        act.wait_ge(qa_rotated, 2 * (j + 1))
                        z_out("f", j, za, f_out)
                    if h == 16:
                        z_out("q", j, zb, q_out)
                    if h == I_END[j]:
                        if j:
                            act.wait_ge(mo_ready, 2 * j)
                        z_out("i", j, val, i_out)
                    if h == OG_END[j]:
                        if j:
                            act.wait_ge(gated, 2 * j)
                        z_out("og", j, eg, og_exp, ACT.Exp, NR)
                    if h == GA_END[j]:
                        act.wait_ge(qa_rotated, 2 * (j + 1))
                        if j:
                            act.wait_ge(gated, 2 * j)
                        z_out("ga", j, eg2, ga_exp, ACT.Exp, NR)
                    if h == OG_END[j] + 1:
                        for t in range(TT):
                            act.wait_ge(og_bounded, 2 * j + t + 1)
                            act.activation(eg[:, t], eg[:, t], ACT.Ln, bias=1.0).then_inc(gate_logs, 1)
                    if h == GA_END[j] + 1:
                        for t in range(TT):
                            act.wait_ge(ga_bounded, 2 * j + t + 1)
                            act.activation(eg2[:, t], eg2[:, t], ACT.Ln, bias=1.0).then_inc(gate_logs, 1)
                    if h == GA_END[j] + 2:
                        for t in range(TT):
                            act.wait_ge(logs_added, 2 * j + t + 1)
                            act.activation(eg[:, t], eg[:, t], ACT.Exp, scale=-1.0).then_inc(gate_sig, 1)
                    for hp in range(2):
                        i = 2 * j + hp
                        if h == F_TURN[hp] + 1:
                            act.wait_ge(full(("fT", j, hp)), nth(("fT", j, hp)))
                            act.activation(hf[:], bank(("fT", j, hp))[:], ACT.Exp, scale=-1.0).then_inc(f_exp, 1)
                        if h == F_TURN[hp] + 2:
                            act.wait_ge(f_bounded, i + 1)
                            chain(act.activation(hf[:], hf[:], ACT.Ln, bias=1.0))
                            act.activation(hf[:], hf[:], ACT.Exp, scale=-1.0).then_inc(f_sig, 1)
                        if h == F_TURN[hp] + 4:
                            act.wait_ge(f_ready, 2 * (i + 1))
                            if i:
                                act.wait_ge(qe_ready, i)
                            act.activation(hg[:], hf[:], ACT.Ln).then_inc(g_ready, 1)
                        if h == Q_TURN[hp] + 1:
                            act.wait_ge(full(("qT", j, hp)), nth(("qT", j, hp)))
                            if i:
                                act.wait_ge(qe_ready, i)
                            act.activation(hq[:], bank(("qT", j, hp))[:], ACT.Exp, scale=-1.0).then_inc(q_exp, 1)
                        if h == Q_TURN[hp] + 2:
                            act.wait_ge(q_bounded, i + 1)
                            chain(act.activation(hq[:], hq[:], ACT.Ln, bias=1.0))
                            act.activation(hq[:], hq[:], ACT.Exp, scale=-1.0).then_inc(q_sig, 1)
                        if h == DECAY[hp]:
                            act.wait_ge(b_ready, i + 1)
                            if i:
                                act.wait_ge(am_masked, i)
                            act.activation(he[:], hd[:], ACT.Exp).then_inc(decays, 1)
                            act.wait_ge(decays, 3 * i + 1)
                            act.activation(hd[:], hd[:], ACT.Exp, scale=-1.0).then_inc(decays, 1)
                            act.activation(hg[:], hb[:], ACT.Exp).then_inc(decays, 1)
                        if h == DECAY[hp] + 2:
                            act.wait_ge(bend_ready, i + 1)
                            act.activation(hf[:], hf[:], ACT.Exp).then_inc(eend_ready, 1)
                        if h == KE_TURN[hp] + 1:
                            act.wait_ge(full(("keT", j, hp)), nth(("keT", j, hp)))
                            if j:
                                act.wait_ge(S_ready, 12 * j)
                            src = bank(("keT", j, hp))[:].rearrange("p (h t c) -> p h t c", h=2, t=2)
                            act.activation(keA[0:CHUNK, 2 * hp:2 * hp + 2], src[0:CHUNK], ACT.Copy)\
                               .then_inc(ke_out, 1)
                            act.activation(keB[CHUNK:P, 2 * hp:2 * hp + 2], src[CHUNK:P, :, 0:1], ACT.Copy)\
                               .then_inc(ke_out, 1)
                    if h == 48:
                        for t in range(TT):
                            act.wait_ge(full(("o", j, t)), nth(("o", j, t)))
                            act.activation((hk if t == 0 else hb)[:], bank(("o", j, t))[:], ACT.Square)\
                               .then_inc(o_squared, 1)
                    if h == 50:
                        rsqrt_start(j + 1, HV, HY, 8)
                    if h == 62:
                        for t in range(TT):
                            i = 2 * j + t
                            act.wait_ge(full(("moT", j, t)), nth(("moT", j, t)))
                            if i >= 2:
                                act.wait_ge(moR_ready, i - 1)
                            act.activation(tmp[:, t], bank(("moT", j, t))[:], ACT.Copy, scale=cols[:, 64:65])\
                               .then_inc(mo_weighted, 1)
                            act.wait_ge(mo_weighted, i + 1)
                            act.activation(mT_hi[:, 0:4, t, :], four(tmp[:, t]), ACT.Copy).then_inc(moR_hi, 1)
                for cb in range(4):
                    if n == WOR + 2 * (cb + 1) + 2:
                        for t in range(TT):
                            x_hi(1, cb, t)
                if n == UP0:
                    act.dma_start(gf_bc[:], g_final.partition_broadcast(P)).then_inc(gf_landed, 16)
                    act.dma_start(pe_sb[:], p[0, 0].rearrange("(t p) n -> p t n", p=P)).then_inc(p_landed, 16)
                for t in range(TT):
                    if n == UP0 + 2 + t:
                        sum_squares(t, 1, u_sb[:, 0].rearrange("p a b -> p (a b)"))
                if n == UP0 + 5:
                    rsqrt_start(NG + 1, V, Y, TT)

            def mlp_steps(slot, r=0):
                kind, j, col = block_before(slot[1], 1)
                if kind == "up" and slot[5] == 0:
                    act.wait_ge(w_used, product(kind, j, col, r))
                    if j == 0 and col == 0:
                        act.wait_ge(r_ready, 2)
                    for t in range(TT):
                        act.activation(u_sb[:, col, t], acc_of(kind, j, col, t)[:], ACT.Relu,
                                       scale=stat[:, R + t:R + t + 1]).then_inc(u_ready, 1)
                if kind == "up" and slot[5] == 3:
                    dst = (aT_hi if j % 2 == 0 else mT_hi)
                    for t in range(TT):
                        i = 2 * (2 * j + col) + t
                        act.wait_ge(full(("uT", j, col, t)), nth(("uT", j, col, t), r))
                        if i >= 2:
                            act.wait_ge(aT_ready, count(i - 1, r, LOOP_TURNS))
                        act.activation(tmp[:, t], bank(("uT", j, col, t))[:], ACT.Square).then_inc(squared, 1)
                        act.wait_ge(squared, count(i + 1, r, LOOP_TURNS))
                        act.activation(dst[:, 4 * col:4 * col + 4, t, :], four(tmp[:, t]), ACT.Copy)\
                           .then_inc(a_hi, 1)

            def tail_steps(n):
                if n == DOWN7 + 1:
                    for t in range(TT):
                        act.wait_ge(full(("ppT", t)), nth(("ppT", t)))
                        act.activation(pT_hi[:, :, t, :],
                                       bank(("ppT", t))[:, 0:2 * P].rearrange("p (k c) -> p k c", k=2), ACT.Copy)\
                           .then_inc(pp_hi, 1)
                for cb in range(4):
                    if n == DOWN7 + 4 * (cb + 1) + 2:
                        for t in range(TT):
                            act.wait_ge(full(("x2T", cb, t)), nth(("x2T", cb, t)))
                            act.activation(hT_hi[:, 4 * cb:4 * cb + 4, t, :], four(bank(("x2T", cb, t))[:]),
                                           ACT.Copy).then_inc(hi_done, 1)
                    if n == PROJ[cb] + 1:
                        act.wait_ge(w_used, product("proj", 0, cb))
                        for t in range(TT):
                            act.activation(pj[:, t, cb * COLS:(cb + 1) * COLS], acc_of("proj", 0, cb, t)[:],
                                           ACT.Copy).then_inc(proj_out, 1)
                    if n == PROJ[cb] + 9:
                        act.wait_ge(w_used, product("gate", 0, cb))
                        if cb:
                            act.wait_ge(x3_ready, 2 * cb)
                        for t in range(TT):
                            act.activation(eple[:, t], acc_of("gate", 0, cb, t)[:], ACT.Sigmoid)\
                               .then_inc(gate_out, 1)
                        if cb == 3:
                            nc.scalar.preload_act_table_set("natural_log_exp_and_others")
                        for t in range(TT):
                            act.wait_ge(x3_ready, 2 * cb + t + 1)
                            act.activation(u_sb[:, 0, 0], x_sb[:, t, cb * COLS:(cb + 1) * COLS], ACT.Square,
                                           accum_out=stat[:, SS + 4 * t + cb:SS + 4 * t + cb + 1])\
                               .then_inc(ss_ready, 1)
                            act.wait_ge(ss_ready, 8 + 2 * cb + t + 1)

            for slot in HEAD:
                if slot[0] in (0, 2, 4, 6):
                    for t in range(TT):
                        x_hi(0, slot[0] // 2, t)
                split_hi(slot)
                act.wait_ge(w_hi_ready, slot[0] + 1)
                n = slot[0] - LAG
                if 0 <= n <= UP0 + 7:
                    steps(n)
                if n >= UP0:
                    mlp_steps(HEAD[n])
            with act.Fori(0, ROUNDS) as r:
                for i, slot in enumerate(BODY):
                    split_hi(slot, r)
                    if i >= LAG:
                        act.wait_ge(w_hi_ready, count(slot[0] + 1, r, LOOP_CHUNKS))
                        mlp_steps(BODY[i - LAG], r)
            for i, slot in enumerate(TAIL):
                split_hi(slot)
                act.wait_ge(w_hi_ready, slot[0] + 1)
                if i >= LAG:
                    tail_steps(slot[0] - LAG)
            for n in range(TAIL[-1][0] - LAG + 1, TAIL[-1][0] + 2):
                tail_steps(n)
            rsqrt_start(NG + 2, V, Y, TT)
            act.wait_ge(r_ready, 3)
            act.wait_ge(x3_scaled, 8)
            act.activation(x_sb[:, 1, 1024:2048], x_sb[:, 1, 1024:2048], ACT.Copy, scale=stat[:, R + 1:R + 2])\
               .then_inc(last_ready, 1)
            act.wait_ge(last_ready, 1)
            act.dma_start(out[0, P:2 * P, 1024:2048], x_sb[:, 1, 1024:2048]).then_inc(out_stored, 16)

        @block.vector
        def _(dve):
            chain = Chain(dve, "dve_chain")

            def split_lo(slot, r=0):
                n = slot[0]
                dve.wait_ge(w_hi_ready, count(n + 1, r, LOOP_CHUNKS))
                dve.tensor_tensor(w_lo[:, n % W_SLOTS], w_raw[:, n % RAW_SLOTS],
                                  w_hi[:, n % W_SLOTS].bitcast(F32), ALU.subtract).then_inc(w_lo_ready, 1)

            def rsqrt_sharpen(which, v, y, out_, scratch, width):
                dve.wait_ge(rs_y, which + 1)
                vs, ys, s = (stat[:, c:c + width] for c in (v, y, scratch))
                chain(dve.tensor_tensor(s, ys, ys, ALU.mult))
                chain(dve.tensor_tensor(s, s, vs, ALU.mult))
                chain(dve.tensor_scalar(s, s, -0.5, 1.5, ALU.mult, ALU.add))
                chain(dve.tensor_tensor(stat[:, out_:out_ + width], s, ys, ALU.mult))

            def row_norm_v(stage):
                dve.wait_ge(ss_ready, (4, 8, 16)[stage])
                parts = stat[:, SS:SS + (8 if stage == 2 else 4)].rearrange("p (t h) -> p t h", t=TT)
                chain(dve.tensor_reduce(stat[:, V:V + 2], parts, AX_X, ALU.add))
                dve.tensor_scalar(stat[:, V:V + 2], stat[:, V:V + 2], 1.0 / D_MODEL, EPS, ALU.mult, ALU.add)\
                   .then_inc(rs_v, 1)

            def row_norm_r(stage, which):
                rsqrt_sharpen(which, V, Y, R, HW, TT)
                dve.tensor_scalar(stat[:, NR:NR + 2], stat[:, R:R + 2], -1.0, None, ALU.mult)\
                   .then_inc(r_ready, 1)

            def x_weighted(stage, cb, t):
                name = ("xT" if stage == 0 else "x1T", cb, t)
                dve.wait_ge(full(name), nth(name))
                i = 8 * stage + 2 * cb + t
                if i >= 2:
                    dve.wait_ge(hT_ready, i - 1)
                g = cols[:, 16 * stage + 4 * cb:16 * stage + 4 * cb + 4].unsqueeze(2).to_broadcast([P, 4, P])
                dve.tensor_tensor(four(tmp[:, t]), four(bank(name)[:]), g, ALU.mult).then_inc(tmp_full, 1)

            def x_lo(stage, cb, t):
                i = 8 * stage + 2 * cb + t
                dve.wait_ge(hi_done, i + 1)
                ks = slice(4 * cb, 4 * cb + 4)
                dve.tensor_tensor(hT_lo[:, ks, t, :], four(tmp[:, t]), hT_hi[:, ks, t, :].bitcast(F32),
                                  ALU.subtract).then_inc(hT_ready, 1)

            def rotate(src, dsts, t, heads, ta, tb):
                c_ = cos[:, t:t + 1, :].to_broadcast([P, heads, 32])
                s_ = sin[:, t:t + 1, :].to_broadcast([P, heads, 32])
                x1, x2 = src[:, :, 0:32], src[:, :, 32:64]
                for half, (ca, cb_, op) in enumerate(((x1, x2, ALU.subtract), (x2, x1, ALU.add))):
                    dve.tensor_tensor(ta, ca, c_, ALU.mult).then_inc(rope_products, 1)
                    dve.tensor_tensor(tb, cb_, s_, ALU.mult).then_inc(rope_products, 1)
                    rope[0] += 2
                    dve.wait_ge(rope_products, rope[0])
                    for d in dsts:
                        chain(dve.tensor_tensor(d[:, :, 32 * half:32 * half + 32], ta, tb, op))

            rope = [0]

            def rope_tables():
                dve.wait_ge(pos_landed, 16)
                dve.wait_ge(invf_made, HD // 2)
                chain(dve.tensor_copy(posf[:], posi[:]))
                w = sgb[:, 1].rearrange("p (q a) -> p q a", q=8)
                ang, whole, kh, s = w[:, 0], w[:, 1], w[:, 2], w[:, 3]
                for t in range(TT):
                    chain(dve.tensor_scalar(ang[:, 32 * t:32 * t + 32], invf[:], posf[:, t:t + 1], None, ALU.mult))
                chain(dve.tensor_scalar(s, ang, 1.0 / TWO_PI, None, ALU.mult))
                chain(dve.tensor_scalar(s, s, ROUND_MAGIC, None, ALU.add))
                chain(dve.tensor_scalar(whole, s, ROUND_MAGIC, None, ALU.subtract))
                chain(dve.tensor_scalar(s, whole, 1.0 / 2048, None, ALU.mult))
                chain(dve.tensor_scalar(s, s, ROUND_MAGIC, None, ALU.add))
                chain(dve.tensor_scalar(s, s, ROUND_MAGIC, None, ALU.subtract))
                chain(dve.tensor_scalar(kh, s, 2048.0, None, ALU.mult))
                chain(dve.tensor_tensor(whole, whole, kh, ALU.subtract))
                for c in (C1, C2, C3):
                    for k in (kh, whole):
                        chain(dve.scalar_tensor_tensor(out=ang, in0=k, scalar=-c, in1=ang, op0=ALU.mult, op1=ALU.add))
                chain(dve.tensor_scalar(sgb[:, 0, 0:64], ang, PI_IN, -PI_IN, ALU.min, ALU.max))
                chain(dve.tensor_scalar(s, sgb[:, 0, 0:64], -1.0, None, ALU.mult))
                chain(dve.tensor_tensor(s, s, sgb[:, 0, 0:64], ALU.max))
                dve.tensor_scalar(sgb[:, 0, 64:128], s, -1.0, float(np.pi / 2), ALU.mult, ALU.add)\
                   .then_inc(angles_ready, 1)

            def lower_bounds_start():
                dve.wait_ge(full(("rows",)), nth(("rows",)))
                dve.tensor_copy(cols[:], bank(("rows",))[:, 0:P]).then_inc(cols_ready, 1)
                dve.wait_ge(cols_ready, 1)
                chain(dve.tensor_tensor(asc[:, 0:16], cols[:, 32:48], cols[:, 48:64], ALU.max))
                chain(dve.tensor_tensor(asc[:, 16:32], cols[:, 32:48], asc[:, 0:16], ALU.subtract))
                dve.tensor_tensor(asc[:, 32:48], cols[:, 48:64], asc[:, 0:16], ALU.subtract)\
                   .then_inc(lbd_ready, 1)

            def lower_bounds_end():
                dve.wait_ge(lb_exp, 1)
                chain(dve.tensor_tensor(asc[:, 0:16], asc[:, 16:32], asc[:, 32:48], ALU.add))
                chain(dve.reciprocal(asc[:, 0:16], asc[:, 0:16]))
                chain(dve.tensor_tensor(lb[:], asc[:, 16:32], asc[:, 0:16], ALU.mult))
                chain(dve.tensor_scalar(one_lb[:], lb[:], -1.0, 1.0, ALU.mult, ALU.add))

            def add_block(kind, j, col, r=0):
                dve.wait_ge(w_used, product(kind, j, col, r))
                for t in range(TT):
                    xs = x_sb[:, t, col * COLS:(col + 1) * COLS]
                    dve.tensor_tensor(xs, acc_of(kind, j, col, t)[:], xs, ALU.add).then_inc(x_added, 1)

            def score_max(j, u, t, pair):
                name = ("score", j, u)
                dve.wait_ge(full(name), nth(name))
                k0, nk = keys_of(t)
                s = bank(name)[:, 0:2 * nk].rearrange("p (v k) -> p v k", v=2)
                for half in range(2):
                    rows_ = slice(half * CHUNK, (half + 1) * CHUNK)
                    first = max(0, (2 * t + half - 1) * CHUNK) - k0
                    end = (2 * t + half + 1) * CHUNK - k0
                    chain(dve.tensor_reduce(asc[rows_, MX:MX + 2], s[rows_, :, first:end], AX_X, ALU.max))
                head = 2 * pair
                if j == 0 and u == 0:
                    dve.wait_ge(sinks_landed, 16)
                sk = sink_bc[:, 8 * j + head:8 * j + head + 2]
                chain(dve.scalar_tensor_tensor(out=asc[:, MX:MX + 2], in0=asc[:, MX:MX + 2], scalar=HD ** -0.5,
                                               in1=sk, op0=ALU.mult, op1=ALU.max))
                dve.tensor_scalar(asc[:, NM + 8 * t + head:NM + 8 * t + head + 2], asc[:, MX:MX + 2], -1.0, None,
                                  ALU.mult).then_inc(nm_ready, 1)

            def attention_gated(j):
                dve.wait_ge(sink_exp, j + 1)
                den = asc[:, DEN:DEN + 16].rearrange("p (t h) -> p t h", t=TT)
                es = asc[:, SD:SD + 16].rearrange("p (t h) -> p t h", t=TT)
                chain(dve.tensor_tensor(den.unsqueeze(3), oa[:, :, :, HD:HD + 1], es.unsqueeze(3), ALU.add))
                chain(dve.reciprocal(asc[:, DEN:DEN + 16], asc[:, DEN:DEN + 16]))
                for t in range(TT):
                    g = sgb[:, t].rearrange("p (h d) -> p h d", h=8)
                    o = oa[:, t, :, 0:HD]
                    chain(dve.tensor_tensor(g, g, den[:, t].unsqueeze(2).to_broadcast([P, 8, HD]), ALU.mult))
                    dve.tensor_tensor(g, g, o, ALU.mult).then_inc(am_ready, 1)

            def steps(n):
                if n == 4:
                    row_norm_v(0)
                if n == 6:
                    row_norm_r(0, 0)
                    lower_bounds_end()
                for t in range(TT):
                    if n == KV1 + 1 + 2 * t:
                        dve.wait_ge(kv_out, 2)
                        dve.wait_ge(trig_ready, 2)
                        dve.wait_ge(zeroed, 8)
                        dst = (gate if t == 0 else eg)[:].rearrange("p a b -> p (a b)")\
                            .rearrange("p (h v c) -> p h v c", h=4, v=2)
                        ta, tb = (zb[:, q, 0:128].rearrange("p (h c) -> p h c", h=4) for q in range(2))
                        rotate(eg2[:, t, 0:256].rearrange("p (h c) -> p h c", h=4),
                               (dst[:, :, 0, 0:HD], dst[:, :, 1, HD:2 * HD]), t, 4, ta, tb)
                        dve.tensor_copy(stat[:, 60:61], stat[:, R:R + 1]).then_inc(k_rotated, 1)
                for j in range(NG):
                    a, h = n - A0[j], n - H0[j]
                    for t in range(TT):
                        if a == -7 + 2 * t:
                            dve.wait_ge(qa_out, 2 * (j + 1))
                            ta, tb = (eg2[:, q, 0:256].rearrange("p (h c) -> p h c", h=8) for q in range(2))
                            rotate(za[:, t].rearrange("p (h c) -> p h c", h=8),
                                   (zb[:, t].rearrange("p (h c) -> p h c", h=8),), t, 8, ta, tb)
                            dve.tensor_copy(stat[:, 61:62], stat[:, R:R + 1]).then_inc(qa_rotated, 1)
                    if a == 0:
                        for t in range(TT):
                            dve.wait_ge(gb_exp, 2 * j + t + 1)
                            dve.tensor_scalar(sgb[:, t], sgb[:, t], E_MAX, None, ALU.min).then_inc(gb_bounded, 1)
                    for u in range(8):
                        t, pair = divmod(u, 4)
                        if a == UNIT * u + 5:
                            score_max(j, u, t, pair)
                        if a == UNIT * u + 8:
                            dve.wait_ge(full(("pT", j, u)), nth(("pT", j, u)))
                            n_ = 2 * (t + 1)
                            dve.tensor_copy(pT[:, 0:n_, :],
                                            bank(("pT", j, u))[:, 0:n_ * P].rearrange("p (k c) -> p k c", k=n_))\
                               .then_inc(pT_out, 1)
                        if a == UNIT * u + 10:
                            dve.wait_ge(full(("pv", j, u)), nth(("pv", j, u)))
                            dve.tensor_copy(oa[:, t, 2 * pair:2 * pair + 2, :],
                                            bank(("pv", j, u))[:, 0:2 * (HD + 1)].rearrange("p (h c) -> p h c", h=2))\
                               .then_inc(pv_out, 1)
                    if a == ATT_END:
                        dve.tensor_tensor(asc[:, SD:SD + 16].rearrange("p (t h) -> p t h", t=TT),
                                          asc[:, NM:NM + 16].rearrange("p (t h) -> p t h", t=TT),
                                          sink_bc[:, 8 * j:8 * j + 8].unsqueeze(1).to_broadcast([P, TT, 8]),
                                          ALU.add).then_inc(sinkd_ready, 1)
                    if a == ATT_END + 2:
                        dve.wait_ge(pv_out, 8 * (j + 1))
                        dve.wait_ge(gb_sig, 2 * (j + 1))
                        attention_gated(j)
                    if a == ATT_END + 5:
                        for t in range(TT):
                            dve.wait_ge(moA_hi, 2 * j + t + 1)
                            dve.tensor_tensor(mT_lo[:, 4:8, t, :], four(bank(("amT", j, t))[:]),
                                              mT_hi[:, 4:8, t, :].bitcast(F32), ALU.subtract)\
                               .then_inc(moA_ready, 1)
                    for hp in range(2):
                        pair_steps(j, hp, h)
                    for c in range(3):
                        if h == (43, 43, 45)[c]:
                            dve.wait_ge(full(("state", j, c)), nth(("state", j, c)))
                            for hh in range(HG):
                                src = bank(("state", j, c))[:, hh * P:(hh + 1) * P]
                                if c == 0:
                                    dve.tensor_copy(Sst[:, 0, hh, :], src).then_inc(S_ready, 1)
                                else:
                                    dve.wait_ge(S_ready, 12 * j + 4 * c)
                                    dve.scalar_tensor_tensor(out=Sst[:, c, hh, :], in0=Sst[:, c - 1, hh, :],
                                                             scalar=ebl[:, hh, c:c + 1], in1=src,
                                                             op0=ALU.mult, op1=ALU.add).then_inc(S_ready, 1)
                    if h == OG_END[j]:
                        dve.wait_ge(og_exp, 2 * (j + 1))
                        if j == 0:
                            dve.wait_ge(kTp_out, 4)
                        for t in range(TT):
                            dve.tensor_scalar(gate[:, t], acc_of("og", j, 0, t)[:], stat[:, R + t:R + t + 1], None,
                                              ALU.mult).then_inc(og_out, 1)
                        for t in range(TT):
                            dve.tensor_scalar(eg[:, t], eg[:, t], E_MAX, None, ALU.min).then_inc(og_bounded, 1)
                    if h == GA_END[j]:
                        for t in range(TT):
                            dve.wait_ge(ga_exp, 2 * j + t + 1)
                            dve.tensor_scalar(eg2[:, t], eg2[:, t], E_MAX, None, ALU.min).then_inc(ga_bounded, 1)
                    if h == 49:
                        for t in range(TT):
                            dve.wait_ge(o_squared, 2 * j + t + 1)
                            chain(dve.tensor_reduce(stat[:, HV + 4 * t:HV + 4 * t + 4],
                                                    four((hk if t == 0 else hb)[:]), AX_X, ALU.add))
                        dve.tensor_scalar(stat[:, HV:HV + 8], stat[:, HV:HV + 8], 1.0 / P, EPS, ALU.mult, ALU.add)\
                           .then_inc(rs_v, 1)
                    if h == GA_END[j] + 1:
                        dve.wait_ge(gate_logs, 4 * (j + 1))
                        for t in range(TT):
                            dve.tensor_tensor(eg[:, t], eg[:, t], eg2[:, t], ALU.add).then_inc(logs_added, 1)
                    if h == GA_END[j] + 2:
                        dve.wait_ge(og_out, 2 * (j + 1))
                        for t in range(TT):
                            dve.wait_ge(gate_sig, 2 * j + t + 1)
                            dve.tensor_tensor(gate[:, t], gate[:, t], eg[:, t], ALU.mult).then_inc(gated, 1)
                    if h == 52:
                        rsqrt_sharpen(j + 1, HV, HY, HR, HW, 8)
                    if h == 60:
                        dve.wait_ge(gated, 2 * (j + 1))
                        for t in range(TT):
                            dve.wait_ge(full(("o", j, t)), nth(("o", j, t)))
                            for hh in range(HG):
                                gs = gate[:, t, hh * P:(hh + 1) * P]
                                ins = dve.scalar_tensor_tensor(
                                    out=gs, in0=bank(("o", j, t))[:, hh * P:(hh + 1) * P],
                                    scalar=stat[:, HR + 4 * t + hh:HR + 4 * t + hh + 1], in1=gs,
                                    op0=ALU.mult, op1=ALU.mult)
                            ins.then_inc(mo_ready, 1)
                    if h == 62:
                        for t in range(TT):
                            dve.wait_ge(moR_hi, 2 * j + t + 1)
                            dve.tensor_tensor(mT_lo[:, 0:4, t, :], four(tmp[:, t]),
                                              mT_hi[:, 0:4, t, :].bitcast(F32), ALU.subtract)\
                               .then_inc(moR_ready, 1)
                    for c in range(4):
                        if j < NG - 1 and n == at(HEAD, "wo", j, c) + 4:
                            add_block("wo", j, c)
                for c in range(4):
                    if n == at(HEAD, "woa", NG - 1, c) + 2:
                        add_block("woa", NG - 1, c)
                    if n == WOR + 2 * (c + 1):
                        add_block("wor", NG - 1, c)
                    if n == WOR + 2 * (c + 1) + 2:
                        for t in range(TT):
                            x_weighted(1, c, t)
                        for t in range(TT):
                            x_lo(1, c, t)
                if n == UP0 + 4:
                    row_norm_v(1)
                if n == UP0 + 6:
                    row_norm_r(1, NG + 1)

            def pair_steps(j, hp, h):
                i = 2 * j + hp
                if h == F_TURN[hp] + 1:
                    dve.wait_ge(f_exp, i + 1)
                    dve.tensor_scalar(hf[:], hf[:], E_MAX, None, ALU.min).then_inc(f_bounded, 1)
                if h == F_TURN[hp] + 3:
                    dve.wait_ge(f_sig, i + 1)
                    for hh in range(2):
                        head = HG * j + 2 * hp + hh
                        fs = hf[:, hh * 256:(hh + 1) * 256]
                        dve.tensor_scalar(fs, fs, one_lb[:, head:head + 1], lb[:, head:head + 1],
                                          ALU.mult, ALU.add).then_inc(f_ready, 1)
                if h == F_TURN[hp] + 4:
                    dve.wait_ge(f_ready, 2 * (i + 1))
                    chain(dve.tensor_scalar(hk[:], hf[:], -1.0, 1.0, ALU.mult, ALU.add))
                if h == F_TURN[hp] + 5:
                    dve.wait_ge(g_ready, i + 1)
                    if i == 0:
                        dve.wait_ge(masks_made, 2)
                    chain(dve.tensor_tensor_scan(hb[:], smask[:], hg[:], 0.0, ALU.mult, ALU.add))
                    b3 = hb[:].rearrange("p (s c) -> p s c", c=CHUNK)
                    dve.tensor_tensor(hd[:].rearrange("p (s c) -> p s c", c=CHUNK), b3,
                                      b3[:, :, CHUNK // 2 - 1:CHUNK // 2].to_broadcast([P, 8, CHUNK]),
                                      ALU.subtract).then_inc(b_ready, 1)
                if h == Q_TURN[hp] + 1:
                    dve.wait_ge(q_exp, i + 1)
                    dve.tensor_scalar(hq[:], hq[:], E_MAX, None, ALU.min).then_inc(q_bounded, 1)
                if h == Q_TURN[hp] + 3:
                    dve.wait_ge(q_sig, i + 1)
                    dve.tensor_tensor(hq[:], bank(("qT", j, hp))[:], hq[:], ALU.mult).then_inc(q_ready, 1)
                if h == DECAY[hp] + 1:
                    dve.wait_ge(decays, 3 * (i + 1))
                    dve.wait_ge(q_ready, i + 1)
                    b3 = hb[:].rearrange("p (s c) -> p s c", c=CHUNK)
                    dve.tensor_tensor(hf[:].rearrange("p (s c) -> p s c", c=CHUNK),
                                      b3[:, :, CHUNK - 1:CHUNK].to_broadcast([P, 8, CHUNK]), b3,
                                      ALU.subtract).then_inc(bend_ready, 1)
                    g3 = hg[:].rearrange("p (h s c) -> p h s c", h=2, c=CHUNK)
                    chain(dve.tensor_copy(ebl[:, 2 * hp:2 * hp + 2, :].unsqueeze(3), g3[:, :, :, CHUNK - 1:CHUNK]))
                    chain(dve.tensor_tensor(he[:], he[:], hq[:], ALU.mult))
                    dve.tensor_tensor(hd[:], hd[:], hk[:], ALU.mult).then_inc(qkd_ready, 1)
                    dve.tensor_tensor(qe[:, 2 * hp:2 * hp + 2, :], hg[:].rearrange("p (h c) -> p h c", h=2),
                                      hq[:].rearrange("p (h c) -> p h c", h=2), ALU.mult).then_inc(qe_ready, 1)
                if h == DECAY[hp] + 3:
                    dve.wait_ge(eend_ready, i + 1)
                    dve.tensor_tensor(hf[:], hf[:], hk[:], ALU.mult).then_inc(ke_ready, 1)
                if h == KE_TURN[hp] + 1:
                    dve.wait_ge(full(("aT", j, hp)), nth(("aT", j, hp)))
                    if i == 0:
                        dve.wait_ge(zeroed, 8)
                    for s0, nt in HALVES:
                        rows_, ts = slice(s0, s0 + HALF), slice(s0, s0 + nt)
                        ins = dve.copy_predicated(
                            am[rows_, hp, :, ts], cmask[rows_, :, ts].bitcast(U32).to_broadcast([HALF, 4, nt]),
                            four(bank(("aT", j, hp))[:])[rows_, :, ts])
                    ins.then_inc(am_masked, 1)

            def mlp_steps(slot, r=0):
                kind, j, col = block_before(slot[1], 1)
                if kind == "down" and slot[5] == 0:
                    add_block(kind, j, col, r)
                if kind == "up" and slot[5] == 3:
                    hi, lo = (aT_hi, aT_lo) if j % 2 == 0 else (mT_hi, mT_lo)
                    ks = slice(4 * col, 4 * col + 4)
                    for t in range(TT):
                        dve.wait_ge(a_hi, count(2 * (2 * j + col) + t + 1, r, LOOP_TURNS))
                        dve.tensor_tensor(lo[:, ks, t, :], four(tmp[:, t]), hi[:, ks, t, :].bitcast(F32),
                                          ALU.subtract).then_inc(aT_ready, 1)

            def tail_steps(n):
                if n == DOWN7:
                    last_of_round()
                if n == DOWN7 + 1:
                    for t in range(TT):
                        dve.wait_ge(pp_hi, t + 1)
                        dve.tensor_tensor(pT_lo[:, :, t, :],
                                          bank(("ppT", t))[:, 0:2 * P].rearrange("p (k c) -> p k c", k=2),
                                          pT_hi[:, :, t, :].bitcast(F32), ALU.subtract).then_inc(ppT_ready, 1)
                for cb in range(4):
                    ks = slice(4 * cb, 4 * cb + 4)
                    cs = slice(cb * COLS, (cb + 1) * COLS)
                    if n == DOWN7 + 4 * (cb + 1):
                        add_block("down", 7, cb)
                    if n == DOWN7 + 4 * (cb + 1) + 2:
                        for t in range(TT):
                            dve.wait_ge(hi_done, 16 + 2 * cb + t + 1)
                            dve.tensor_tensor(hT_lo[:, ks, t, :], four(bank(("x2T", cb, t))[:]),
                                              hT_hi[:, ks, t, :].bitcast(F32), ALU.subtract)\
                               .then_inc(hT_ready, 1)
                    if n == PROJ[cb] + 9:
                        for t in range(TT):
                            dve.wait_ge(gate_out, 2 * cb + t + 1)
                            dve.wait_ge(proj_out, 2 * (cb + 1))
                            chain(dve.tensor_tensor(eple[:, t], eple[:, t], pj[:, t, cs], ALU.mult))
                            dve.tensor_tensor(x_sb[:, t, cs], x_sb[:, t, cs], eple[:, t], ALU.add)\
                               .then_inc(x3_ready, 1)
                    if n == PROJ[cb] + 10 and cb < 3:
                        x3_times_g(cb)

            def x3_times_g(cb):
                cs = slice(cb * COLS, (cb + 1) * COLS)
                dve.wait_ge(gf_landed, 16)
                for t in range(TT):
                    dve.wait_ge(ss_ready, 8 + 2 * cb + t + 1)
                    dve.tensor_tensor(x_sb[:, t, cs], x_sb[:, t, cs], gf_bc[:, cs], ALU.mult).then_inc(x3_scaled, 1)

            def last_of_round():
                dve.wait_ge(w_used, TAIL_CHUNKS0)
                for t in range(TT):
                    xs = x_sb[:, t, 3 * COLS:4 * COLS]
                    a = acc[(TAIL_BLOCKS0 - 1) % 2][t]
                    dve.tensor_tensor(xs, a[:], xs, ALU.add).then_inc(x_added, 1)

            rope_tables()
            lower_bounds_start()
            for slot in HEAD:
                if slot[0] in (0, 2, 4, 6):
                    for t in range(TT):
                        x_weighted(0, slot[0] // 2, t)
                    for t in range(TT):
                        x_lo(0, slot[0] // 2, t)
                split_lo(slot)
                dve.wait_ge(w_lo_ready, slot[0] + 1)
                n = slot[0] - LAG
                if 0 <= n <= UP0 + 7:
                    steps(n)
                if n > UP0:
                    mlp_steps(HEAD[n])
            with dve.Fori(0, ROUNDS) as r:
                for i, slot in enumerate(BODY):
                    split_lo(slot, r)
                    if i >= LAG:
                        dve.wait_ge(w_lo_ready, count(slot[0] + 1, r, LOOP_CHUNKS))
                        mlp_steps(BODY[i - LAG], r)
            for i, slot in enumerate(TAIL):
                split_lo(slot)
                dve.wait_ge(w_lo_ready, slot[0] + 1)
                if i >= LAG:
                    tail_steps(slot[0] - LAG)
            for n in range(TAIL[-1][0] - LAG + 1, TAIL[-1][0] + 2):
                tail_steps(n)
            row_norm_v(2)
            x3_times_g(3)
            row_norm_r(2, NG + 2)
            dve.wait_ge(r_ready, 3)
            dve.wait_ge(x3_scaled, 8)
            for t, half in OUT_PARTS:
                hs = slice(half * 1024, (half + 1) * 1024)
                dve.tensor_scalar(x_sb[:, t, hs], x_sb[:, t, hs], stat[:, R + t:R + t + 1], None, ALU.mult)\
                   .then_inc(out_ready, 1)


_INS = ["x", "p", "positions", "g_mix", "w_in", "lb_logits", "hgrn_norm_g", "sinks", "w_out",
        "g_mlp", "w_up", "w_down", "w_ple_gate", "w_ple_proj", "g_final"]
_OUT = ((1, 256, 2048), "float32")


def kernel(**inputs):
    import concourse.bacc as bacc
    from concourse.bass_utils import run_bass_kernel_spmd

    nc = bacc.Bacc("TRN2", target_bir_lowering=False, num_devices=1)
    arrays, args = {}, []
    for name in _INS:
        a = np.ascontiguousarray(inputs[name])
        arrays[f"in_{name}_dram"] = a
        args.append(nc.dram_tensor(f"in_{name}_dram", a.shape, mybir.dt.from_np(a.dtype), kind="ExternalInput").ap())
    out = nc.dram_tensor("out_dram", _OUT[0], mybir.dt.float32, kind="ExternalOutput").ap()
    program(nc, *args, out)
    result = run_bass_kernel_spmd(nc, [arrays], core_ids=[0])
    return result.results[0]["out_dram"]
```
